# Optimizing a Trainium2 kernel written in Bass

```python
import jax, jax.numpy as jnp
from jax import lax
import numpy as np

D_MODEL = 2048
BATCH = 1
SEQ = 256
DEPTH = 1

MEM_LEN = 256
ATTN_HEADS = 8
HEAD_DIM = 128
ATTN_WIDTH = ATTN_HEADS * HEAD_DIM
CONV_WIDTH = D_MODEL // 2
MIX_WIDTH = ATTN_WIDTH + CONV_WIDTH
IN_WIDTH = 3 * ATTN_WIDTH + 3 * CONV_WIDTH
CONV_K = 3
MOBA_BLOCK = 256
MOBA_TOPK = 3
Q_CHUNK = 16
XATTN_HEADS = 4
XATTN_HEAD_DIM = 128
XATTN_WIDTH = XATTN_HEADS * XATTN_HEAD_DIM
D_FF = ((int(8 * D_MODEL / 3) + 255) // 256) * 256
RMS_EPS = 1e-6
NEG = -1e30

kernel_name = "hymba_moba_shortconv_macaron"

def rmsnorm(x, g):
    xf = x.astype(jnp.float32)
    y = xf * lax.rsqrt(jnp.mean(xf * xf, axis=-1, keepdims=True) + RMS_EPS)
    return (y * g.astype(jnp.float32)).astype(x.dtype)

def swiglu(x, w_gate, w_up, w_down):
    return (jax.nn.silu(x @ w_gate) * (x @ w_up)) @ w_down

def moba_attention(q, k, v):
    b, s, h, dh = q.shape
    n_blk = -(-s // MOBA_BLOCK)
    s_pad = n_blk * MOBA_BLOCK
    pad = ((0, 0), (0, s_pad - s), (0, 0), (0, 0))
    q, k, v = [jnp.pad(t, pad).transpose(0, 2, 1, 3) for t in (q, k, v)]
    scale = dh ** -0.5
    kb = k.reshape(b, h, n_blk, MOBA_BLOCK, dh)
    vb = v.reshape(b, h, n_blk, MOBA_BLOCK, dh)
    topk = min(MOBA_TOPK, n_blk - 1)
    n_chunk = s_pad // Q_CHUNK
    qc = q.reshape(b, h, n_chunk, Q_CHUNK, dh).transpose(2, 0, 1, 3, 4)
    xs = (jnp.arange(n_chunk, dtype=jnp.int32), qc)
    if topk > 0:
        k_mean = jnp.mean(kb.astype(jnp.float32), axis=3)
        gate = jnp.einsum('bhsd,bhnd->bhsn', q.astype(jnp.float32), k_mean)
        q_blk = jnp.arange(s_pad, dtype=jnp.int32) // MOBA_BLOCK
        past = jnp.arange(n_blk, dtype=jnp.int32)[None, :] < q_blk[:, None]
        gate = jnp.where(past, gate, NEG)
        _, idx = lax.top_k(gate, topk)
        valid = idx < q_blk[:, None]
        idx_c = idx.reshape(b, h, n_chunk, Q_CHUNK, topk).transpose(2, 0, 1, 3, 4)
        valid_c = valid.reshape(b, h, n_chunk, Q_CHUNK, topk).transpose(2, 0, 1, 3, 4)
        xs = xs + (idx_c, valid_c)
    bi = jnp.arange(b)[:, None, None, None]
    hi = jnp.arange(h)[None, :, None, None]

    def chunk_attend(xs_i):
        c, q_i = xs_i[0], xs_i[1]
        t = c * Q_CHUNK + jnp.arange(Q_CHUNK, dtype=jnp.int32)
        blk = (c * Q_CHUNK) // MOBA_BLOCK
        k_own = lax.dynamic_index_in_dim(kb, blk, axis=2, keepdims=False)
        v_own = lax.dynamic_index_in_dim(vb, blk, axis=2, keepdims=False)
        qf = q_i.astype(jnp.float32) * scale
        s_own = jnp.einsum('bhqd,bhpd->bhqp', qf, k_own.astype(jnp.float32))
        kpos = blk * MOBA_BLOCK + jnp.arange(MOBA_BLOCK, dtype=jnp.int32)
        s_own = jnp.where(kpos[None, :] <= t[:, None], s_own, NEG)
        if topk > 0:
            idx_i, valid_i = xs_i[2], xs_i[3]
            k_sel = kb[bi, hi, idx_i]
            v_sel = vb[bi, hi, idx_i]
            s_sel = jnp.einsum('bhqd,bhqkpd->bhqkp', qf, k_sel.astype(jnp.float32))
            s_sel = jnp.where(valid_i[..., None], s_sel, NEG)
            s_sel = s_sel.reshape(b, h, Q_CHUNK, topk * MOBA_BLOCK)
            p = jax.nn.softmax(jnp.concatenate([s_own, s_sel], axis=-1), axis=-1)
            p_own = p[..., :MOBA_BLOCK]
            p_sel = p[..., MOBA_BLOCK:].reshape(b, h, Q_CHUNK, topk, MOBA_BLOCK)
            o = (jnp.einsum('bhqp,bhpd->bhqd', p_own, v_own.astype(jnp.float32))
                 + jnp.einsum('bhqkp,bhqkpd->bhqd', p_sel, v_sel.astype(jnp.float32)))
        else:
            p = jax.nn.softmax(s_own, axis=-1)
            o = jnp.einsum('bhqp,bhpd->bhqd', p, v_own.astype(jnp.float32))
        return o.astype(q_i.dtype)

    out = lax.map(chunk_attend, xs)
    out = out.transpose(1, 0, 3, 2, 4).reshape(b, s_pad, h, dh)
    return out[:, :s]

def short_conv(u, w):
    return lax.conv_general_dilated(
        u, w[:, None, :].astype(u.dtype), window_strides=(1,), padding=((CONV_K - 1, 0),),
        dimension_numbers=('NWC', 'WIO', 'NWC'), feature_group_count=u.shape[-1])

def cross_attention(n, m, w_q, w_kv, w_o):
    b, s, _ = n.shape
    ml = m.shape[1]
    qx = (n @ w_q).reshape(b, s, XATTN_HEADS, XATTN_HEAD_DIM)
    kx, vx = jnp.split(m @ w_kv, 2, axis=-1)
    kx = kx.reshape(b, ml, XATTN_HEADS, XATTN_HEAD_DIM)
    vx = vx.reshape(b, ml, XATTN_HEADS, XATTN_HEAD_DIM)
    sc = jnp.einsum('bshd,bmhd->bhsm', qx.astype(jnp.float32), kx.astype(jnp.float32)) * (XATTN_HEAD_DIM ** -0.5)
    p = jax.nn.softmax(sc, axis=-1)
    o = jnp.einsum('bhsm,bmhd->bshd', p, vx.astype(jnp.float32)).astype(n.dtype)
    return o.reshape(b, s, XATTN_WIDTH) @ w_o

def setup_inputs(seed: int = 0) -> dict:
    key = jax.random.key(seed)
    ks = jax.random.split(key, 24)
    L, D, F = DEPTH, D_MODEL, D_FF
    nrm = lambda k, shape, fan_in: jax.random.normal(k, shape, jnp.float32) * (fan_in ** -0.5)
    gain = lambda k, shape: 1.0 + 0.02 * jax.random.normal(k, shape, jnp.float32)
    return {
        "x": jax.random.normal(ks[0], (BATCH, SEQ, D), jnp.float32),
        "mem": jax.random.normal(ks[1], (BATCH, MEM_LEN, D), jnp.float32),
        "ffn1_norm": gain(ks[2], (L, D)),
        "ffn1_w_gate": nrm(ks[3], (L, D, F), D),
        "ffn1_w_up": nrm(ks[4], (L, D, F), D),
        "ffn1_w_down": nrm(ks[5], (L, F, D), F),
        "mix_norm": gain(ks[6], (L, D)),
        "w_in": nrm(ks[7], (L, D, IN_WIDTH), D),
        "conv_w": nrm(ks[8], (L, CONV_K, CONV_WIDTH), CONV_K),
        "attn_out_norm": gain(ks[9], (L, ATTN_WIDTH)),
        "conv_out_norm": gain(ks[10], (L, CONV_WIDTH)),
        "w_out": nrm(ks[11], (L, MIX_WIDTH, D), MIX_WIDTH),
        "xattn_norm": gain(ks[12], (L, D)),
        "mem_norm": gain(ks[13], (L, D)),
        "xattn_w_q": nrm(ks[14], (L, D, XATTN_WIDTH), D),
        "xattn_w_kv": nrm(ks[15], (L, D, 2 * XATTN_WIDTH), D),
        "xattn_w_o": nrm(ks[16], (L, XATTN_WIDTH, D), XATTN_WIDTH),
        "ffn2_norm": gain(ks[17], (L, D)),
        "ffn2_w_gate": nrm(ks[18], (L, D, F), D),
        "ffn2_w_up": nrm(ks[19], (L, D, F), D),
        "ffn2_w_down": nrm(ks[20], (L, F, D), F),
        "final_norm": gain(ks[21], (D,)),
    }

def reference(x, mem, ffn1_norm, ffn1_w_gate, ffn1_w_up, ffn1_w_down, mix_norm, w_in, conv_w,
              attn_out_norm, conv_out_norm, w_out, xattn_norm, mem_norm, xattn_w_q, xattn_w_kv,
              xattn_w_o, ffn2_norm, ffn2_w_gate, ffn2_w_up, ffn2_w_down, final_norm):
    b, s, _ = x.shape
    A, C = ATTN_WIDTH, CONV_WIDTH
    h = x
    for l in range(DEPTH):
        h = h + 0.5 * swiglu(rmsnorm(h, ffn1_norm[l]), ffn1_w_gate[l], ffn1_w_up[l], ffn1_w_down[l])
        n = rmsnorm(h, mix_norm[l])
        proj = n @ w_in[l]
        q, k, v, c_gate, b_gate, u = jnp.split(proj, [A, 2 * A, 3 * A, 3 * A + C, 3 * A + 2 * C], axis=-1)
        hs = (b, s, ATTN_HEADS, HEAD_DIM)
        a_out = moba_attention(q.reshape(hs), k.reshape(hs), v.reshape(hs)).reshape(b, s, A)
        c_out = b_gate * short_conv(c_gate * u, conv_w[l])
        mixed = jnp.concatenate([rmsnorm(a_out, attn_out_norm[l]), rmsnorm(c_out, conv_out_norm[l])], axis=-1)
        h = h + mixed @ w_out[l]
        h = h + cross_attention(rmsnorm(h, xattn_norm[l]), rmsnorm(mem, mem_norm[l]),
                                xattn_w_q[l], xattn_w_kv[l], xattn_w_o[l])
        h = h + 0.5 * swiglu(rmsnorm(h, ffn2_norm[l]), ffn2_w_gate[l], ffn2_w_up[l], ffn2_w_down[l])
    return rmsnorm(h, final_norm)


_drawn_inputs = setup_inputs


def setup_inputs(seed=0):
    import zlib

    import numpy as np

    out = dict(_drawn_inputs(seed))
    spreads = {}
    factors = {'ffn1_norm': 4.814,
     'attn_out_norm': 5.751,
     'conv_out_norm': 5.818,
     'xattn_norm': 8.0,
     'mem_norm': 8.0,
     'ffn2_norm': 8.0,
     'final_norm': 2.763}
    for name, (base, spread) in spreads.items():
        noise = np.random.default_rng([zlib.crc32(name.encode()), seed]).standard_normal(out[name].shape)
        drawn = base * np.exp(spread * noise) if base else spread * noise
        out[name] = __import__('jax').numpy.asarray(drawn.astype(out[name].dtype))
    for name, factor in factors.items():
        out[name] = (out[name] * factor).astype(out[name].dtype)
    return out
```

```python
def build_program(nc, x, mem, gains, final_gain, ffn1_gate, ffn1_up, ffn1_down, w_in, w_out,
                  xattn_q, xattn_kv, xattn_o, ffn2_gate, ffn2_up, ffn2_down, out):
    import concourse.bass as bass
    from concourse import mybir
    from contextlib import ExitStack

    f32, f32r = mybir.dt.float32, mybir.dt.float32r
    ALU, ACT, AX = mybir.AluOpType, mybir.ActivationFunctionType, mybir.AxisListType

    P = 128
    S, D = x.shape
    F = ffn1_gate.shape[1]
    NB = 512
    TT = S // P
    KC = NB // P
    DK = D // P
    DB = D // NB
    FB = F // NB
    AH = w_in.shape[1] // 6 // P
    XH = xattn_q.shape[1] // P
    AW = AH * P
    CT = AW // P
    SCALE = float(P) ** -0.5
    EPS = 1e-6
    NEG = -1e30

    G_FFN1, G_MIX, G_MEM, G_X, G_FFN2 = (DK * j for j in range(5))
    G_ATT = 5 * DK
    G_CONV = G_ATT + AH
    G_TAPS = G_CONV + CT
    N_FFN1, N_MIX, N_MEM, N_X, N_FFN2, N_FINAL, N_ATT, N_CONV = range(8)

    LEAD, RING = 2, 3
    PERIOD = 3 * DB
    STEPS = FB - 1
    C_FFN1 = 0
    C_MEMK = C_FFN1 + 2 * DB + PERIOD * STEPS
    C_DOWN1 = C_MEMK + DB
    C_MEMV = C_DOWN1 + DB
    C_MIX = C_MEMV + DB
    MIX_UNITS = w_in.shape[1] // NB
    C_OUTC = C_MIX + MIX_UNITS * DB
    C_OUTA = C_OUTC + 2 * DB
    C_XQ = C_OUTA + 2 * DB
    C_XO = C_XQ + DB
    C_FFN2 = C_XO + DB
    C_DOWN2 = C_FFN2 + 2 * DB + PERIOD * STEPS
    CHUNKS = C_DOWN2 + DB
    C_HEADS = C_OUTC - DB

    Q_X = 0
    Q_MEM = Q_X + 2 * DB
    Q_T1 = Q_MEM + 2 * DB
    Q_MIX = Q_T1 + 2 * FB
    Q_XN = Q_MIX + 2 * DB
    Q_N2 = Q_XN + 2 * DB
    Q_T2 = Q_N2 + 2 * DB

    MIX_COLS = [(3 * AW, "c"), (5 * AW, "u"), (4 * AW, "b"), (0, "q"), (AW, "k"), (2 * AW, "v")]
    mix_units = [(col + j * NB, kind, j) for col, kind in MIX_COLS for j in range(AW // NB)]

    ctx = ExitStack()
    with ctx:
        at = [(nc.sbuf_base + 31) // 32 * 32]

        def place(name, shape, dt=f32, offset=None):
            size = 2 if dt == mybir.dt.bfloat16 else 4
            for n in shape[1:]:
                size *= n
            if offset is None:
                offset = at[0]
                at[0] += (size + 31) // 32 * 32
            return nc.alloc_sbuf_tensor_at(name, shape, dt, offset=offset)

        w_raw = place("w_raw", [P, RING, KC, NB])
        w_hi = place("w_hi", [P, RING, KC, NB], f32r)
        w_lo = place("w_lo", [P, RING, KC, NB], f32r)
        h = place("h", [P, TT, D])
        nt_hi = place("nt_hi", [P, DK, S], f32r)
        nt_lo = place("nt_lo", [P, DK, S], f32r)
        mt_hi = place("mt_hi", [P, DK, S], f32r)
        mt_lo = place("mt_lo", [P, DK, S], f32r)
        kxT = place("kxT", [P, XH, S])
        vx = place("vx", [P, TT, XH * P])
        ident = place("ident", [P, P])
        ones = place("ones", [P, P])
        mask = place("mask", [P, 3, P])
        gain = place("gain", [P, G_TAPS + 3 * CT])
        squares = place("squares", [P, 8, TT, DB])
        var = place("var", [P, 8, TT])
        root = place("root", [P, 8, TT])
        rinv0 = place("rinv0", [P, 8, TT])
        newt = place("newt", [P, 8, TT])
        newt2 = place("newt2", [P, 8, TT])
        rstd = place("rstd", [P, 8, TT])
        xscale = place("xscale", [P, TT])
        HN = AH + XH
        smax = place("smax", [P, HN, TT])
        sbias = place("sbias", [P, HN, TT])
        ssum = place("ssum", [P, HN, TT])
        sinv = place("sinv", [P, HN, TT])
        base = at[0]
        KB = 1024
        silu_g = place("silu_g", [P, TT, NB], offset=base)
        hidden = place("hidden", [P, TT, NB], offset=base + 4 * KB)
        at_hi = place("at_hi", [P, KC, S], f32r, offset=base + 8 * KB)
        at_lo = place("at_lo", [P, KC, S], f32r, offset=base + 12 * KB)
        m = place("m", [P, TT, D], offset=base + 16 * KB)
        gbc = place("gbc", [P, D], offset=base + 16 * KB)
        cu = place("cu", [P, CT, S], offset=base)
        v = place("v", [P, TT, AW], offset=base)
        co = place("co", [P, CT, S], offset=base + 8 * KB)
        sq_a = place("sq_a", [P, AH, S], offset=base + 8 * KB)
        qT = place("qT", [P, AH, S], offset=base + 16 * KB)
        qxT = place("qxT", [P, XH, S], offset=base + 16 * KB)
        kT = place("kT", [P, AH, S], offset=base + 24 * KB)
        pr = place("pr", [P, 2, TT, S], offset=base + 32 * KB)
        pT = place("pT", [P, 2, TT * S], offset=base + 36 * KB)
        diag = place("diag", [P, TT, P], offset=base + 32 * KB)
        rb = place("rb", [P, S], offset=base + 33 * KB)
        rb2 = place("rb2", [P, S], offset=base + 34 * KB)
        junk = place("junk", [P, NB], mybir.dt.bfloat16, offset=base + 40 * KB)
        assert base + 41 * KB <= nc.sbuf_usable_end, (base + 41 * KB, nc.sbuf_usable_end)

        pair = [ctx.enter_context(nc.psum_tensor(f"pair{p}", [P, 2 * NB], f32)) for p in range(3)]
        tbank = [ctx.enter_context(nc.psum_tensor(f"tbank{b}", [P, NB], f32)) for b in range(2)]
        hbank = [pair[2][:, 0:NB], pair[2][:, NB:2 * NB], tbank[0][:, :], tbank[1][:, :]]

        def sem(name):
            return ctx.enter_context(nc.semaphore(name))

        x_in = [sem(f"x_in{d}") for d in range(DB)]
        mem_in = sem("mem_in")
        gain_in = sem("gain_in")
        gbc_in = sem("gbc_in")
        consts = sem("consts")
        raw_in = [sem(f"raw_in{s}") for s in range(RING)]
        hi_ready = sem("hi_ready")
        lo_ready = sem("lo_ready")
        chunk_done = sem("chunk_done")
        t_put = sem("t_put")
        t_hi = sem("t_hi")
        t_lo = sem("t_lo")
        gate_ready = sem("gate_ready")
        hidden_ready = sem("hidden_ready")
        h_ready = sem("h_ready")
        sq_ready = sem("sq_ready")
        var_ready = sem("var_ready")
        root_ready = sem("root_ready")
        rstd_ready = sem("rstd_ready")
        diag_ready = sem("diag_ready")
        rb_put = sem("rb_put")
        rb_ready = sem("rb_ready")
        ss_put = sem("ss_put")
        dve_step = sem("dve_step")
        cu_ready = sem("cu_ready")
        tap_ready = sem("tap_ready")
        co_ready = sem("co_ready")
        co_hi = sem("co_hi")
        co_lo = sem("co_lo")
        qk_ready = sem("qk_ready")
        v_ready = sem("v_ready")
        memk_ready = sem("memk_ready")
        memv_ready = sem("memv_ready")
        qx_ready = sem("qx_ready")
        s_put = sem("s_put")
        s_bias = sem("s_bias")
        p_exp = sem("p_exp")
        p_ready = sem("p_ready")
        pT_put = sem("pT_put")
        pT_ready = sem("pT_ready")
        o_put = sem("o_put")
        o_hi = sem("o_hi")
        o_lo = sem("o_lo")
        y_ready = sem("y_ready")
        y_out = sem("y_out")

        GATE_PAIR, UP_PAIR = 0, 1
        DOWN_PAIRS = [2, 0, 1, 2]
        MEMK_PAIR, DOWN1_PAIRS, MEMV_PAIR = 0, [2, 1, 0, 2], 1
        XQ_PAIR = 0
        DOWN2_PAIRS = [0, 1, 2, 0]

        block = ctx.enter_context(nc.Block())

        def chunks_to(place_, more=0):
            c, i = place_
            return c + more + PERIOD * i

        @block.sync
        def _(sp):
            def load(c, i, w, row, col):
                if c >= RING:
                    sp.wait_ge(lo_ready, chunks_to((c, i), 1 - RING))
                src = w[row, col].rearrange("(k p) n -> p k n", p=P)
                sp.dma_start(w_raw[:, c % RING], src).then_inc(raw_in[c % RING], 16)

            def rows(c):
                return slice(c * NB, (c + 1) * NB)

            def ffn_loads(c0, gate, up, down):
                for k in range(DB):
                    if c0 == 0:
                        sp.dma_start(h[:, :, rows(k)], x[:, rows(k)].rearrange("(t p) n -> p t n", p=P)
                                     ).then_inc(x_in[k], 16)
                        if k == 0:
                            sp.dma_start(gain[:, :], gains).then_inc(gain_in, 16)
                    load(c0 + k, 0, gate, rows(k), rows(0))
                    if c0 == 0 and k == DB - 1:
                        sp.dma_start(m[:, :, :], mem.rearrange("(t p) n -> p t n", p=P)
                                     ).then_inc(mem_in, 16)
                for k in range(DB):
                    load(c0 + DB + k, 0, up, rows(k), rows(0))
                with sp.Fori(0, STEPS) as i:
                    c = c0 + 2 * DB
                    for k in range(DB):
                        load(c + k, i, gate, rows(k), bass.ds(i * NB + NB, NB))
                    for k in range(DB):
                        load(c + DB + k, i, up, rows(k), bass.ds(i * NB + NB, NB))
                    for d in range(DB):
                        load(c + 2 * DB + d, i, down, bass.ds(i * NB, NB), rows(d))

            ffn_loads(C_FFN1, ffn1_gate, ffn1_up, ffn1_down)
            for k in range(DB):
                load(C_MEMK + k, 0, xattn_kv, rows(k), rows(0))
            for d in range(DB):
                load(C_DOWN1 + d, 0, ffn1_down, rows(FB - 1), rows(d))
            for k in range(DB):
                load(C_MEMV + k, 0, xattn_kv, rows(k), rows(1))
            for u, (col, _, _) in enumerate(mix_units):
                for k in range(DB):
                    load(C_MIX + u * DB + k, 0, w_in, rows(k), slice(col, col + NB))
            for d in range(DB):
                for e in range(2):
                    load(C_OUTC + 2 * d + e, 0, w_out, rows(2 + e), rows(d))
            for d in range(DB):
                for e in range(2):
                    load(C_OUTA + 2 * d + e, 0, w_out, rows(e), rows(d))
            for k in range(DB):
                load(C_XQ + k, 0, xattn_q, rows(k), rows(0))
            for d in range(DB):
                load(C_XO + d, 0, xattn_o, rows(0), rows(d))
            ffn_loads(C_FFN2, ffn2_gate, ffn2_up, ffn2_down)
            sp.wait_ge(o_lo, HN)
            sp.dma_start(gbc[:, :], final_gain.partition_broadcast(P)).then_inc(gbc_in, 16)
            for d in range(DB):
                load(C_DOWN2 + d, 0, ffn2_down, rows(FB - 1), rows(d))
            n = 0
            for t in range(TT):
                for e in range(2):
                    n += 1
                    sp.wait_ge(y_ready, n)
                    cols = slice(e * D // 2, (e + 1) * D // 2)
                    sp.dma_start(out[t * P:(t + 1) * P, cols], h[:, t, cols]).then_inc(y_out, 16)
            sp.wait_ge(y_out, 16 * n)

        @block.gpsimd
        def _(pool):
            nc.gpsimd.memset(ones[:, :], 1.0).then_inc(consts, 1)
            nc.gpsimd.memset(mask[:, :, :], 0.0).then_inc(consts, 1)
            pool.wait_ge(consts, 2)
            nc.gpsimd.affine_select(out=ident[:, :], in_=ones[:, :], compare_op=ALU.is_equal, fill=0.0,
                                    base=0, pattern=[[-1, P]], channel_multiplier=1).then_inc(consts, 1)
            for b in (0, 2):
                nc.gpsimd.affine_select(out=mask[:, b, :], in_=mask[:, b, :], compare_op=ALU.is_ge, fill=NEG,
                                        base=0, pattern=[[-1, P]], channel_multiplier=1).then_inc(consts, 1)

        CONSTS = 5

        @block.tensor
        def _(pe):
            def operand_ready(c, i):
                pe.wait_ge(lo_ready, chunks_to((c, i), 1))

            def tokens_chunk(c, i, p, left, k0, first, last):
                operand_ready(c, i)
                s = c % RING
                for k in range(KC):
                    for t in range(TT):
                        o = pair[p][:, t * NB:(t + 1) * NB]
                        l_hi = left[0][:, k0 + k, t * P:(t + 1) * P]
                        l_lo = left[1][:, k0 + k, t * P:(t + 1) * P]
                        a, z = first and k == 0, last and k == KC - 1
                        nc.tensor.matmul(o, l_hi, w_hi[:, s, k], start=a, stop=False)
                        nc.tensor.matmul(o, l_hi, w_lo[:, s, k], start=False, stop=False)
                        done = nc.tensor.matmul(o, l_lo, w_hi[:, s, k], start=False, stop=z)
                done.then_inc(chunk_done, 1)

            def columns_chunk(c, p, right, first, last):
                operand_ready(c, 0)
                s = c % RING
                for k in range(KC):
                    for j in range(KC):
                        o = pair[p][:, j * S:(j + 1) * S]
                        cols = slice(j * P, (j + 1) * P)
                        kk = right[2] + k
                        a = first and k == 0 and j % 2 == 0
                        z = last and k == KC - 1
                        nc.tensor.matmul(o, w_hi[:, s, k, cols], right[0][:, kk], start=a, stop=False,
                                         skip_group_check=True)
                        nc.tensor.matmul(o, w_lo[:, s, k, cols], right[0][:, kk], start=False, stop=False,
                                         skip_group_check=True)
                        done = nc.tensor.matmul(o, w_hi[:, s, k, cols], right[1][:, kk], start=False, stop=z,
                                                skip_group_check=True)
                done.then_inc(chunk_done, 1)

            NT, MT, AT = (nt_hi, nt_lo), (mt_hi, mt_lo), (at_hi, at_lo)

            def columns_unit(c0, p, right, waits=None):
                for k in range(DB):
                    if waits:
                        waits(k)
                    columns_chunk(c0 + k, p, (*right, k * KC), k == 0, k == DB - 1)
                    yield k

            def transpose_bank(q, i, src, cols):
                if q >= 2:
                    pe.wait_ge(t_lo, q - 1 + 2 * i)
                for j in range(2):
                    for t in range(TT):
                        last = nc.tensor.transpose(
                            tbank[q % 2][:, j * S + t * P:j * S + (t + 1) * P],
                            src[:, t, (cols + j) * P:(cols + j + 1) * P], ident[:, :])
                last.then_inc(t_put, 1)

            def prep(q0, d, src=None):
                for b in range(2):
                    transpose_bank(q0 + 2 * d + b, 0, h if src is None else src, d * KC + 2 * b)

            def transpose_hidden(q, i=0):
                for b in range(2):
                    transpose_bank(q + b, i, hidden, 2 * b)

            def prep_h(q0, d, adds):
                pe.wait_ge(h_ready, adds)
                prep(q0, d)

            def spread_rstd(n):
                pe.wait_ge(diag_ready, n)
                for t in range(TT):
                    last = nc.tensor.matmul(tbank[0][:, t * P:(t + 1) * P], ones[:, :], diag[:, t],
                                            start=True, stop=True)
                last.then_inc(rb_put, 1)

            def sum_squares(sq, n):
                for t in range(TT):
                    for k in range(n):
                        last = nc.tensor.matmul(hbank[0][:, t:t + 1], sq[:, k, t * P:(t + 1) * P],
                                                ones[:, 0:1], start=(k == 0), stop=(k == n - 1))
                last.then_inc(ss_put, 1)

            def scores(hd):
                b = hbank[hd % 4]
                if hd >= 4:
                    pe.wait_ge(o_lo, hd - 3)
                if hd < AH:
                    nc.tensor.matmul(b[:, 0:P], qT[:, hd, 0:P], kT[:, hd, 0:P], start=True, stop=True)
                    last = nc.tensor.matmul(b[:, P:P + S], qT[:, hd, P:S], kT[:, hd, :], start=True, stop=True)
                else:
                    for t in range(TT):
                        last = nc.tensor.matmul(b[:, t * S:(t + 1) * S], qxT[:, hd - AH, t * P:(t + 1) * P],
                                                kxT[:, hd - AH, :], start=True, stop=True)
                last.then_inc(s_put, 1)

            CAUSAL = [(0, 0, 0), (1, 0, P), (1, 1, 2 * P)]
            FULL = [(0, 0, 0), (1, 0, P), (0, 1, 2 * P), (1, 1, 3 * P)]

            def transpose_probs(hd):
                pe.wait_ge(p_ready, hd + 1)
                for t, k, to in (CAUSAL if hd < AH else FULL):
                    last = nc.tensor.transpose(hbank[hd % 4][:, to:to + P],
                                               pr[:, hd % 2, t, k * P:(k + 1) * P], ident[:, :])
                last.then_inc(pT_put, 1)

            def head_out(hd):
                pe.wait_ge(pT_ready, hd + 1)
                b, t = hbank[hd % 4], pT[:, hd % 2]
                if hd < AH:
                    cols = slice(hd * P, (hd + 1) * P)
                    nc.tensor.matmul(b[:, 0:P], v[:, 0, cols], t[:, 0:P], start=True, stop=True)
                    nc.tensor.matmul(b[:, P:S], v[:, 0, cols], t[:, P:S], start=True, stop=False)
                    last = nc.tensor.matmul(b[:, P:S], v[:, 1, cols], t[:, S:S + P], start=False, stop=True)
                else:
                    cols = slice((hd - AH) * P, (hd - AH + 1) * P)
                    nc.tensor.matmul(b[:, 0:S], vx[:, 0, cols], t[:, 0:S], start=True, stop=False)
                    last = nc.tensor.matmul(b[:, 0:S], vx[:, 1, cols], t[:, S:2 * S], start=False, stop=True)
                last.then_inc(o_put, 1)

            def ffn_unit(c0, i, p, waits=None):
                for k in range(DB):
                    if waits:
                        waits(k)
                    tokens_chunk(c0 + k, i, p, NT, k * KC, k == 0, k == DB - 1)
                    yield k

            def ffn_down(c0, i, q, pairs):
                pe.wait_ge(t_lo, q + 2 + 2 * i)
                for d in range(DB):
                    tokens_chunk(c0 + d, i, pairs[d], AT, 0, True, True)
                    yield d

            def drained(steps):
                for _ in steps:
                    pass

            def ffn_loop(c0, q0):
                with pe.Fori(0, STEPS) as i:
                    drained(ffn_unit(c0, i, GATE_PAIR))
                    pe.wait_ge(hidden_ready, hidden_base[0] + 1 + i)
                    transpose_hidden(q0, i)
                    drained(ffn_unit(c0 + DB, i, UP_PAIR))
                    drained(ffn_down(c0 + 2 * DB, i, q0, DOWN_PAIRS))
                pe.wait_ge(hidden_ready, hidden_base[0] + FB)
                transpose_hidden(q0 + 2 * STEPS)
                hidden_base[0] += FB

            hidden_base = [0]

            pe.wait_ge(consts, CONSTS)
            for d in range(2):
                pe.wait_ge(x_in[d], 16)
                prep(Q_X, d)
            for k in ffn_unit(C_FFN1, 0, GATE_PAIR, lambda k: pe.wait_ge(t_lo, Q_X + 2 * k + 2)):
                if k < 2:
                    pe.wait_ge(x_in[2 + k], 16)
                    prep(Q_X, 2 + k)
            for k in ffn_unit(C_FFN1 + DB, 0, UP_PAIR):
                if k == 0:
                    pe.wait_ge(mem_in, 16)
                prep(Q_MEM, k, m)
            ffn_loop(C_FFN1 + 2 * DB, Q_T1)
            for k in columns_unit(C_MEMK, MEMK_PAIR, MT):
                if k == 1:
                    pe.wait_ge(t_lo, Q_MIX)
                    spread_rstd(1)
            for d in ffn_down(C_DOWN1, 0, Q_MIX - 2, DOWN1_PAIRS):
                if d == 1:
                    pe.wait_ge(rb_ready, 1)
                if d > 0:
                    prep_h(Q_MIX, d - 1, DB * (FB - 1) + d)
            for k in range(DB):
                tokens_chunk(C_MEMV + k, 0, MEMV_PAIR, MT, k * KC, k == 0, k == DB - 1)
                if k == 0:
                    prep_h(Q_MIX, DB - 1, DB * FB)
                if k == 1:
                    pe.wait_ge(t_lo, Q_MIX + 2 * DB)
                    spread_rstd(2)
            pe.wait_ge(t_lo, Q_MIX + 2 * DB)
            def head_insert(slot):
                if 2 <= slot < AH + 2:
                    if slot == 2:
                        pe.wait_ge(v_ready, 1)
                    if slot == 2 + AH // 2:
                        pe.wait_ge(v_ready, 2)
                    head_out(slot - 2)
                if 1 <= slot < AH + 1:
                    transpose_probs(slot - 1)
                if slot < AH:
                    if slot == 0:
                        pe.wait_ge(qk_ready, 4)
                        pe.wait_ge(var_ready, 4)
                    scores(slot)

            for u, (_, kind, j) in enumerate(mix_units):
                c0, p = C_MIX + u * DB, u % 2
                if kind == "v":
                    for k in range(DB):
                        tokens_chunk(c0 + k, 0, p, NT, k * KC, k == 0, k == DB - 1)
                        if c0 + k >= C_HEADS:
                            head_insert(c0 + k - C_HEADS)
                else:
                    for k in columns_unit(c0, p, NT):
                        if (kind, j, k) == ("q", 0, 1):
                            pe.wait_ge(co_hi, 2)
                            sum_squares(cu, CT)
            pe.wait_ge(co_lo, 2)
            for d in range(DB):
                p = d % 2
                for e in range(2):
                    c = C_OUTC + 2 * d + e
                    tokens_chunk(c, 0, p, MT, AH + e * KC, e == 0, e == 1)
                    head_insert(c - C_HEADS)
                    if c == C_OUTA - 2:
                        pe.wait_ge(o_lo, AH)
                        sum_squares(sq_a, AH)
            for d in range(DB):
                p = d % 2
                for e in range(2):
                    tokens_chunk(C_OUTA + 2 * d + e, 0, p, MT, e * KC, e == 0, e == 1)
                    if d > 0 and e == 0:
                        prep_h(Q_XN, d - 1, DB * (FB + 1) + d)
            for k in columns_unit(C_XQ, XQ_PAIR, NT, lambda k: pe.wait_ge(t_lo, Q_XN + 2 * k + 2)):
                if k == 0:
                    prep_h(Q_XN, DB - 1, DB * (FB + 2))
            pe.wait_ge(qx_ready, 1)
            pe.wait_ge(memk_ready, 1)
            pe.wait_ge(memv_ready, 1)
            pe.wait_ge(var_ready, 5)
            for hd in range(AH, HN):
                scores(hd)
            for hd in range(AH, HN):
                transpose_probs(hd)
                if hd > AH:
                    head_out(hd - 1)
            head_out(HN - 1)
            pe.wait_ge(o_lo, HN)
            for d in range(DB):
                tokens_chunk(C_XO + d, 0, DOWN_PAIRS[d], MT, 0, True, True)
                if d > 0:
                    prep_h(Q_N2, d - 1, DB * (FB + 2) + d)
            for k in ffn_unit(C_FFN2, 0, GATE_PAIR, lambda k: pe.wait_ge(t_lo, Q_N2 + 2 * k + 2)):
                if k == 0:
                    prep_h(Q_N2, DB - 1, DB * (FB + 3))
            drained(ffn_unit(C_FFN2 + DB, 0, UP_PAIR))
            ffn_loop(C_FFN2 + 2 * DB, Q_T2)
            drained(ffn_down(C_DOWN2, 0, Q_T2 + 2 * STEPS, DOWN2_PAIRS))

        @block.scalar
        def _(act):
            sums = [0]

            def split(c, i=0):
                if c >= CHUNKS:
                    return
                act.wait_ge(raw_in[c % RING], 16 * (c // RING + 1) + 16 * PERIOD // RING * i)
                if c >= RING:
                    act.wait_ge(chunk_done, chunks_to((c, i), 1 - RING))
                nc.scalar.copy(w_hi[:, c % RING], w_raw[:, c % RING]).then_inc(hi_ready, 1)

            def chunk_over(c, i=0):
                act.wait_ge(chunk_done, chunks_to((c, i), 1))

            def bank_out(q, i, dst, k0, g=None):
                act.wait_ge(t_put, q + 1 + 2 * i)
                src = tbank[q % 2]
                if g is None:
                    last = nc.scalar.copy(dst[:, k0:k0 + 2, :], src[:, :].rearrange("p (k s) -> p k s", k=2))
                else:
                    for j in range(2):
                        last = nc.scalar.activation(dst[:, k0 + j, :], src[:, j * S:(j + 1) * S], ACT.Identity,
                                                    scale=gain[:, g + k0 + j:g + k0 + j + 1])
                last.then_inc(t_hi, 1)

            def prep_out(q0, d, dst, g):
                for b in range(2):
                    bank_out(q0 + 2 * d + b, 0, dst, d * KC + 2 * b, g)

            def hidden_out(q, i=0):
                for b in range(2):
                    bank_out(q + b, i, at_hi, 2 * b)

            def square_sums(norm, d, src):
                for t in range(TT):
                    if sums[0] >= 1:
                        act.wait_ge(sq_ready, sums[0])
                    nc.scalar.activation(junk[:, :], src[:, t, d * NB:(d + 1) * NB], ACT.Square,
                                         accum_out=squares[:, norm, t, d:d + 1]).then_inc(sq_ready, 1)
                    sums[0] += 1

            roots = [0]

            def square_root(norm):
                roots[0] += 1
                act.wait_ge(var_ready, roots[0])
                nc.scalar.activation(root[:, norm], var[:, norm], ACT.Sqrt).then_inc(root_ready, 1)

            def gate_out(c, i, b):
                chunk_over(c, i)
                if not (isinstance(b, int) and b == 0):
                    act.wait_ge(hidden_ready, b)
                for t in range(TT):
                    last = nc.scalar.activation(silu_g[:, t], pair[GATE_PAIR][:, t * NB:(t + 1) * NB], ACT.Silu,
                                                scale=rstd[:, ffn_norm[0], t:t + 1])
                last.then_inc(gate_ready, 1)

            ffn_norm = [N_FFN1]

            def ffn_loop(c0, q0, b0):
                with act.Fori(0, STEPS) as i:
                    for k in range(PERIOD):
                        split(c0 + k + LEAD, i)
                        if k == DB - 1:
                            hidden_out(q0, i)
                            gate_out(c0 + k, i, b0 + 1 + i)

            def head_exp(hd):
                act.wait_ge(s_bias, hd + 1)
                b = hbank[hd % 4]
                if hd < AH:
                    parts = [(0, b[:, 0:P], P), (1, b[:, P:P + S], S)]
                else:
                    parts = [(t, b[:, t * S:(t + 1) * S], S) for t in range(TT)]
                if hd >= 2:
                    act.wait_ge(pT_put, hd - 1)
                for t, s, n in parts:
                    last = nc.scalar.activation(pr[:, hd % 2, t, 0:n], s, ACT.Exp, bias=sbias[:, hd, t:t + 1],
                                                scale=SCALE if hd < AH else xscale[:, t:t + 1],
                                                accum_out=ssum[:, hd, t:t + 1])
                last.then_inc(p_exp, 1)

            def head_probs_out(hd):
                act.wait_ge(pT_put, hd + 1)
                if hd >= 2:
                    act.wait_ge(o_put, hd - 1)
                n = S + P if hd < AH else 2 * S
                nc.scalar.copy(pT[:, hd % 2, 0:n], hbank[hd % 4][:, 0:n]).then_inc(pT_ready, 1)

            def head_out(hd):
                act.wait_ge(o_put, hd + 1)
                if hd < AH:
                    nc.scalar.activation(sq_a[:, hd, :], hbank[hd % 4][:, 0:S], ACT.Square)
                    nc.scalar.activation(mt_hi[:, hd, :], hbank[hd % 4][:, 0:S], ACT.Identity,
                                         scale=gain[:, G_ATT + hd:G_ATT + hd + 1]).then_inc(o_hi, 1)
                else:
                    nc.scalar.copy(mt_hi[:, hd - AH, :], hbank[hd % 4][:, 0:S]).then_inc(o_hi, 1)

            def head_post(slot):
                if 2 <= slot < AH + 2:
                    head_out(slot - 2)
                if 1 <= slot < AH + 1:
                    head_probs_out(slot - 1)
                if slot < AH:
                    head_exp(slot)

            act.wait_ge(gain_in, 16)
            for d in range(2):
                prep_out(Q_X, d, nt_hi, G_FFN1)
            for c in range(LEAD):
                split(c)
            for k in range(DB):
                split(C_FFN1 + k + LEAD)
                if k < 2:
                    prep_out(Q_X, 2 + k, nt_hi, G_FFN1)
                    for d in (2 * k, 2 * k + 1):
                        act.wait_ge(x_in[d], 16)
                        square_sums(N_FFN1, d, h)
                if k == 2:
                    square_root(N_FFN1)
                if k == DB - 1:
                    act.wait_ge(rstd_ready, 1)
                    gate_out(C_FFN1 + k, 0, 0)
            for k in range(DB):
                split(C_FFN1 + DB + k + LEAD)
                prep_out(Q_MEM, k, mt_hi, G_MEM)
                act.wait_ge(mem_in, 16)
                square_sums(N_MEM, k, m)
            ffn_loop(C_FFN1 + 2 * DB, Q_T1, 0)
            hidden_out(Q_MIX - 2)
            for k in range(DB):
                split(C_MEMK + k + LEAD)
                if k == 0:
                    square_root(N_MEM)
            for d in range(DB):
                split(C_DOWN1 + d + LEAD)
                if d > 0:
                    prep_out(Q_MIX, d - 1, nt_hi, G_MIX)
                act.wait_ge(h_ready, DB * (FB - 1) + d + 1)
                square_sums(N_MIX, d, h)
            for k in range(DB):
                split(C_MEMV + k + LEAD)
                if k == 0:
                    prep_out(Q_MIX, DB - 1, nt_hi, G_MIX)
                    square_root(N_MIX)
            chunk_over(C_MIX - 1)
            act.wait_ge(rstd_ready, 2)
            for t in range(TT):
                last = nc.scalar.activation(vx[:, t, :], pair[MEMV_PAIR][:, t * NB:(t + 1) * NB], ACT.Identity,
                                            scale=rstd[:, N_MEM, t:t + 1])
            last.then_inc(memv_ready, 1)
            for u, (_, kind, j) in enumerate(mix_units):
                c0, p = C_MIX + u * DB, u % 2
                for k in range(DB):
                    c = c0 + k
                    split(c + LEAD)
                    if (kind, j, k) == ("q", 0, 1):
                        square_root(N_CONV)
                    if k == DB - 1 and kind == "u":
                        act.wait_ge(cu_ready, j + 1)
                        for n in range(KC):
                            ch = j * KC + n
                            tap = gain[:, G_TAPS + 2 * CT + ch:G_TAPS + 2 * CT + ch + 1]
                            last = nc.scalar.activation(co[:, ch, :], cu[:, ch, :], ACT.Identity, scale=tap)
                        last.then_inc(tap_ready, 1)
                    if k == DB - 1 and kind == "b":
                        act.wait_ge(co_ready, j + 1)
                        for n in range(KC):
                            ch = j * KC + n
                            nc.scalar.activation(mt_hi[:, AH + ch, :], co[:, ch, :], ACT.Identity,
                                                 scale=gain[:, G_CONV + ch:G_CONV + ch + 1])
                        nc.scalar.activation(cu[:, j * KC:(j + 1) * KC, :], co[:, j * KC:(j + 1) * KC, :],
                                             ACT.Square).then_inc(co_hi, 1)
                    if k == DB - 1 and kind == "v":
                        chunk_over(c)
                        if j == 0:
                            act.wait_ge(ss_put, 1)
                            act.wait_ge(rstd_ready, 3)
                        for t in range(TT):
                            last = nc.scalar.activation(v[:, t, j * NB:(j + 1) * NB],
                                                        pair[p][:, t * NB:(t + 1) * NB], ACT.Identity,
                                                        scale=rstd[:, N_MIX, t:t + 1])
                        last.then_inc(v_ready, 1)
                    if c >= C_HEADS:
                        if c == C_HEADS + 2:
                            act.wait_ge(co_lo, 2)
                        head_post(c - C_HEADS)
            for c in range(C_OUTC, C_OUTA):
                split(c + LEAD)
                head_post(c - C_HEADS)
                if c == C_OUTA - 2:
                    square_root(N_ATT)
            for d in range(DB):
                for e in range(2):
                    split(C_OUTA + 2 * d + e + LEAD)
                    if d > 0 and e == 0:
                        prep_out(Q_XN, d - 1, nt_hi, G_X)
                act.wait_ge(h_ready, DB * (FB + 1) + d + 1)
                square_sums(N_X, d, h)
            for k in range(DB):
                split(C_XQ + k + LEAD)
                if k == 0:
                    prep_out(Q_XN, DB - 1, nt_hi, G_X)
                    square_root(N_X)
            chunk_over(C_XO - 1)
            nc.scalar.copy(qxT[:, :, :], pair[XQ_PAIR][:, :].rearrange("p (k s) -> p k s", k=XH)).then_inc(qx_ready, 1)
            for hd in range(AH, HN):
                head_exp(hd)
                if hd > AH:
                    head_probs_out(hd - 1)
                if hd > AH + 1:
                    head_out(hd - 2)
            head_probs_out(HN - 1)
            head_out(HN - 2)
            head_out(HN - 1)
            for d in range(DB):
                split(C_XO + d + LEAD)
                if d > 0:
                    prep_out(Q_N2, d - 1, nt_hi, G_FFN2)
                act.wait_ge(h_ready, DB * (FB + 2) + d + 1)
                square_sums(N_FFN2, d, h)
            ffn_norm[0] = N_FFN2
            for k in range(DB):
                split(C_FFN2 + k + LEAD)
                if k == 0:
                    prep_out(Q_N2, DB - 1, nt_hi, G_FFN2)
                    square_root(N_FFN2)
                if k == DB - 1:
                    act.wait_ge(rstd_ready, 7)
                    gate_out(C_FFN2 + k, 0, FB)
            for k in range(DB):
                split(C_FFN2 + DB + k + LEAD)
            ffn_loop(C_FFN2 + 2 * DB, Q_T2, FB)
            hidden_out(Q_T2 + 2 * STEPS)
            for d in range(DB):
                split(C_DOWN2 + d + LEAD)
                act.wait_ge(h_ready, DB * (2 * FB + 2) + d + 1)
                square_sums(N_FINAL, d, h)
            square_root(N_FINAL)

        @block.vector
        def _(dve):
            steps = [0]
            norms = [0]

            def own(ins, signal=None, value=None):
                if signal is None:
                    steps[0] += 1
                    signal, value = dve_step, steps[0]
                ins.then_inc(signal, 1)
                dve.wait_ge(signal, value)

            def split(c, i=0):
                if c >= CHUNKS:
                    return
                dve.wait_ge(hi_ready, chunks_to((c, i), 1))
                nc.vector.tensor_tensor(w_lo[:, c % RING], w_raw[:, c % RING], w_hi[:, c % RING],
                                        ALU.subtract).then_inc(lo_ready, 1)

            def chunk_over(c, i=0):
                dve.wait_ge(chunk_done, chunks_to((c, i), 1))

            def bank_out(q, i, hi, lo, k0, g=None):
                dve.wait_ge(t_hi, q + 1 + 2 * i)
                src = tbank[q % 2]
                if g is None:
                    last = nc.vector.tensor_tensor(lo[:, k0:k0 + 2, :], src[:, :].rearrange("p (k s) -> p k s", k=2),
                                                   hi[:, k0:k0 + 2, :], ALU.subtract)
                else:
                    for j in range(2):
                        last = nc.vector.scalar_tensor_tensor(
                            lo[:, k0 + j, :], src[:, j * S:(j + 1) * S], gain[:, g + k0 + j:g + k0 + j + 1],
                            hi[:, k0 + j, :], ALU.mult, ALU.subtract)
                last.then_inc(t_lo, 1)

            def prep_out(q0, d, hi, lo, g):
                for b in range(2):
                    bank_out(q0 + 2 * d + b, 0, hi, lo, d * KC + 2 * b, g)

            def hidden_out(q, i=0):
                for b in range(2):
                    bank_out(q + b, i, at_hi, at_lo, 2 * b)

            def rms(norm, width, sums=None, puts=None, spread=False):
                if sums is not None:
                    dve.wait_ge(sq_ready, sums)
                    own(nc.vector.reduce_sum(newt[:, norm], squares[:, norm], AX.X))
                    src = newt[:, norm]
                else:
                    dve.wait_ge(ss_put, puts)
                    src = hbank[0][:, 0:TT]
                norms[0] += 1
                nc.vector.tensor_scalar(var[:, norm], src, 1.0 / width, EPS, ALU.mult,
                                        ALU.add).then_inc(var_ready, 1)
                dve.wait_ge(root_ready, norms[0])
                dve.wait_ge(var_ready, norms[0])
                own(nc.vector.reciprocal(rinv0[:, norm], root[:, norm]))
                own(nc.vector.tensor_tensor(newt2[:, norm], rinv0[:, norm], rinv0[:, norm], ALU.mult))
                own(nc.vector.scalar_tensor_tensor(root[:, norm], newt2[:, norm], -0.5, var[:, norm],
                                                   ALU.mult, ALU.mult))
                nc.vector.scalar_tensor_tensor(rstd[:, norm], root[:, norm], 1.5, rinv0[:, norm],
                                               ALU.add, ALU.mult).then_inc(rstd_ready, 1)
                dve.wait_ge(rstd_ready, norms[0])
                if spread:
                    for t in range(TT):
                        last = nc.vector.tensor_scalar(diag[:, t], ident[:, :], rstd[:, norm, t:t + 1], None,
                                                       ALU.mult)
                    last.then_inc(diag_ready, 1)

            def add_to_h(c, i, d, p, scale):
                chunk_over(c, i)
                cols = slice(d * NB, (d + 1) * NB)
                if isinstance(scale, float):
                    nc.vector.scalar_tensor_tensor(
                        h[:, :, cols], pair[p][:, :].rearrange("p (t n) -> p t n", t=TT), scale, h[:, :, cols],
                        ALU.mult, ALU.add).then_inc(h_ready, 1)
                else:
                    for t in range(TT):
                        last = nc.vector.scalar_tensor_tensor(
                            h[:, t, cols], pair[p][:, t * NB:(t + 1) * NB], scale[:, t:t + 1], h[:, t, cols],
                            ALU.mult, ALU.add)
                    last.then_inc(h_ready, 1)

            def hidden_block(c, i, b):
                chunk_over(c, i)
                dve.wait_ge(gate_ready, b + 1)
                for t in range(TT):
                    last = nc.vector.scalar_tensor_tensor(
                        hidden[:, t], pair[UP_PAIR][:, t * NB:(t + 1) * NB], rstd[:, ffn_norm[0], t:t + 1],
                        silu_g[:, t], ALU.mult, ALU.mult)
                last.then_inc(hidden_ready, 1)

            ffn_norm = [N_FFN1]

            def ffn_loop(c0, q0, b0):
                with dve.Fori(0, STEPS) as i:
                    for k in range(PERIOD):
                        split(c0 + k + LEAD, i)
                        if k == DB - 1:
                            hidden_out(q0, i)
                        if k == 2 * DB - 1:
                            hidden_block(c0 + k, i, b0 + 1 + i)
                        if k >= 2 * DB:
                            d = k - 2 * DB
                            add_to_h(c0 + k, i, d, DOWN_PAIRS[d], 0.5)

            def columns_of(p):
                return pair[p][:, :].rearrange("p (k s) -> p k s", k=KC)

            def over_rms(which):
                return which[:, :].unsqueeze(1).to_broadcast([P, KC, S])

            def head_bias(hd):
                dve.wait_ge(s_put, hd + 1)
                b = hbank[hd % 4]
                if hd < AH:
                    own(nc.vector.tensor_tensor(b[:, 0:3 * P], b[:, 0:3 * P],
                                                mask[:, :, :].rearrange("p a b -> p (a b)"), ALU.add))
                    nc.vector.reduce_max(smax[:, hd, 0:1], b[:, 0:P], AX.X)
                    own(nc.vector.reduce_max(smax[:, hd, 1:2], b[:, P:P + S], AX.X))
                    nc.vector.tensor_scalar(sbias[:, hd], smax[:, hd], -SCALE, None, ALU.mult).then_inc(s_bias, 1)
                else:
                    own(nc.vector.reduce_max(smax[:, hd], b[:, 0:2 * S].rearrange("p (t s) -> p t s", t=TT), AX.X))
                    nc.vector.scalar_tensor_tensor(sbias[:, hd], smax[:, hd], -1.0, xscale[:, :],
                                                   ALU.mult, ALU.mult).then_inc(s_bias, 1)

            def head_probs(hd):
                dve.wait_ge(p_exp, hd + 1)
                own(nc.vector.reciprocal(sinv[:, hd], ssum[:, hd]))
                for t in range(TT):
                    n = P if (hd < AH and t == 0) else S
                    last = nc.vector.tensor_scalar(pr[:, hd % 2, t, 0:n], pr[:, hd % 2, t, 0:n],
                                                   sinv[:, hd, t:t + 1], None, ALU.mult)
                last.then_inc(p_ready, 1)

            def head_out(hd):
                dve.wait_ge(o_hi, hd + 1)
                if hd < AH:
                    nc.vector.scalar_tensor_tensor(mt_lo[:, hd, :], hbank[hd % 4][:, 0:S],
                                                   gain[:, G_ATT + hd:G_ATT + hd + 1], mt_hi[:, hd, :],
                                                   ALU.mult, ALU.subtract).then_inc(o_lo, 1)
                else:
                    nc.vector.tensor_tensor(mt_lo[:, hd - AH, :], hbank[hd % 4][:, 0:S], mt_hi[:, hd - AH, :],
                                            ALU.subtract).then_inc(o_lo, 1)

            def head_post(slot):
                if slot < AH:
                    head_bias(slot)
                if 2 <= slot < AH + 2:
                    head_out(slot - 2)
                if slot < AH:
                    head_probs(slot)

            dve.wait_ge(gain_in, 16)
            for d in range(2):
                prep_out(Q_X, d, nt_hi, nt_lo, G_FFN1)
            for c in range(LEAD):
                split(c)
            for k in range(DB):
                split(C_FFN1 + k + LEAD)
                if k < 2:
                    prep_out(Q_X, 2 + k, nt_hi, nt_lo, G_FFN1)
                if k == 2:
                    rms(N_FFN1, D, TT * DB)
            for k in range(DB):
                split(C_FFN1 + DB + k + LEAD)
                prep_out(Q_MEM, k, mt_hi, mt_lo, G_MEM)
            hidden_block(C_FFN1 + 2 * DB - 1, 0, 0)
            ffn_loop(C_FFN1 + 2 * DB, Q_T1, 0)
            hidden_out(Q_MIX - 2)
            for k in range(DB):
                split(C_MEMK + k + LEAD)
                if k == 0:
                    rms(N_MEM, D, 2 * TT * DB, spread=True)
                if k == 1:
                    dve.wait_ge(rb_put, 1)
                    own(nc.vector.tensor_copy(rb[:, :], tbank[0][:, 0:S]), rb_ready, 1)
            chunk_over(C_DOWN1 - 1)
            nc.vector.tensor_tensor(kxT[:, :, :], columns_of(MEMK_PAIR), over_rms(rb),
                                    ALU.mult).then_inc(memk_ready, 1)
            for d in range(DB):
                split(C_DOWN1 + d + LEAD)
                add_to_h(C_DOWN1 + d, 0, d, DOWN1_PAIRS[d], 0.5)
                if d > 0:
                    prep_out(Q_MIX, d - 1, nt_hi, nt_lo, G_MIX)
            for k in range(DB):
                split(C_MEMV + k + LEAD)
                if k == 0:
                    prep_out(Q_MIX, DB - 1, nt_hi, nt_lo, G_MIX)
                    rms(N_MIX, D, 3 * TT * DB, spread=True)
                if k == 1:
                    dve.wait_ge(rb_put, 2)
                    own(nc.vector.tensor_copy(rb[:, :], tbank[0][:, 0:S]), rb_ready, 2)
                    own(nc.vector.tensor_tensor(rb2[:, :], rb[:, :], rb[:, :], ALU.mult))
            for u, (_, kind, j) in enumerate(mix_units):
                c0, p, blk = C_MIX + u * DB, u % 2, slice(j * KC, (j + 1) * KC)
                for k in range(DB):
                    c = c0 + k
                    split(c + LEAD)
                    if (kind, j, k) == ("q", 0, 1):
                        rms(N_CONV, CT * P, puts=1)
                    if c >= C_HEADS:
                        head_post(c - C_HEADS)
                if kind != "v":
                    chunk_over(c0 + DB - 1)
                if kind == "c":
                    own(nc.vector.tensor_tensor(cu[:, blk, :], columns_of(p), over_rms(rb2), ALU.mult))
                if kind == "u":
                    nc.vector.tensor_tensor(cu[:, blk, :], columns_of(p), cu[:, blk, :],
                                            ALU.mult).then_inc(cu_ready, 1)
                    dve.wait_ge(tap_ready, j + 1)
                    for back in (1, 2):
                        for n in range(KC):
                            ch = j * KC + n
                            col = G_TAPS + (2 - back) * CT + ch
                            last = nc.vector.scalar_tensor_tensor(
                                co[:, ch, back:S], cu[:, ch, 0:S - back], gain[:, col:col + 1],
                                co[:, ch, back:S], ALU.mult, ALU.add)
                        own(last)
                if kind == "b":
                    own(nc.vector.tensor_tensor(cu[:, blk, :], columns_of(p), over_rms(rb), ALU.mult))
                    nc.vector.tensor_tensor(co[:, blk, :], co[:, blk, :], cu[:, blk, :],
                                            ALU.mult).then_inc(co_ready, 1)
                    dve.wait_ge(co_hi, j + 1)
                    for n in range(KC):
                        ch = j * KC + n
                        last = nc.vector.scalar_tensor_tensor(
                            mt_lo[:, AH + ch, :], co[:, ch, :], gain[:, G_CONV + ch:G_CONV + ch + 1],
                            mt_hi[:, AH + ch, :], ALU.mult, ALU.subtract)
                    last.then_inc(co_lo, 1)
                if kind in ("q", "k"):
                    nc.vector.tensor_tensor((qT if kind == "q" else kT)[:, blk, :], columns_of(p), over_rms(rb),
                                            ALU.mult).then_inc(qk_ready, 1)
            for d in range(DB):
                for e in range(2):
                    c = C_OUTC + 2 * d + e
                    split(c + LEAD)
                    head_post(c - C_HEADS)
                    if c == C_OUTA - 2:
                        rms(N_ATT, AW, puts=2)
                add_to_h(c, 0, d, d % 2, rstd[:, N_CONV])
            for d in range(DB):
                for e in range(2):
                    c = C_OUTA + 2 * d + e
                    split(c + LEAD)
                    if d > 0 and e == 0:
                        prep_out(Q_XN, d - 1, nt_hi, nt_lo, G_X)
                add_to_h(c, 0, d, d % 2, rstd[:, N_ATT])
            for k in range(DB):
                split(C_XQ + k + LEAD)
                if k == 0:
                    prep_out(Q_XN, DB - 1, nt_hi, nt_lo, G_X)
                    rms(N_X, D, 4 * TT * DB)
                    own(nc.vector.tensor_scalar(xscale[:, :], rstd[:, N_X], SCALE, None, ALU.mult))
            for hd in range(AH, HN):
                head_bias(hd)
                if hd > AH:
                    head_probs(hd - 1)
                if hd > AH + 1:
                    head_out(hd - 2)
            head_probs(HN - 1)
            head_out(HN - 2)
            head_out(HN - 1)
            for d in range(DB):
                split(C_XO + d + LEAD)
                add_to_h(C_XO + d, 0, d, DOWN_PAIRS[d], 1.0)
                if d > 0:
                    prep_out(Q_N2, d - 1, nt_hi, nt_lo, G_FFN2)
            ffn_norm[0] = N_FFN2
            for k in range(DB):
                split(C_FFN2 + k + LEAD)
                if k == 0:
                    prep_out(Q_N2, DB - 1, nt_hi, nt_lo, G_FFN2)
                    rms(N_FFN2, D, 5 * TT * DB)
            for k in range(DB):
                split(C_FFN2 + DB + k + LEAD)
            hidden_block(C_FFN2 + 2 * DB - 1, 0, FB)
            ffn_loop(C_FFN2 + 2 * DB, Q_T2, FB)
            hidden_out(Q_T2 + 2 * STEPS)
            for d in range(DB):
                split(C_DOWN2 + d + LEAD)
                add_to_h(C_DOWN2 + d, 0, d, DOWN2_PAIRS[d], 0.5)
            rms(N_FINAL, D, 6 * TT * DB)
            dve.wait_ge(gbc_in, 16)
            dve.wait_ge(h_ready, DB * (2 * FB + 3))
            for t in range(TT):
                for e in range(2):
                    cols = slice(e * D // 2, (e + 1) * D // 2)
                    nc.vector.scalar_tensor_tensor(h[:, t, cols], h[:, t, cols], rstd[:, N_FINAL, t:t + 1],
                                                   gbc[:, cols], ALU.mult, ALU.mult).then_inc(y_ready, 1)


def kernel(**inputs):
    import numpy as np
    import concourse.bacc as bacc
    from concourse import mybir
    from concourse.bass_utils import run_bass_kernel_spmd

    def features(a):
        a = np.asarray(a)
        a = a.reshape(-1, a.shape[-1] // 128, 128)
        return a.transpose(2, 0, 1).reshape(128, -1)

    gains = np.concatenate([features(inputs[n]) for n in (
        "ffn1_norm", "mix_norm", "mem_norm", "xattn_norm", "ffn2_norm", "attn_out_norm", "conv_out_norm",
        "conv_w")], axis=1)
    arrays = {
        "x": inputs["x"][0], "mem": inputs["mem"][0], "gains": gains, "final_gain": inputs["final_norm"],
        "ffn1_gate": inputs["ffn1_w_gate"][0], "ffn1_up": inputs["ffn1_w_up"][0],
        "ffn1_down": inputs["ffn1_w_down"][0], "w_in": inputs["w_in"][0], "w_out": inputs["w_out"][0],
        "xattn_q": inputs["xattn_w_q"][0], "xattn_kv": inputs["xattn_w_kv"][0], "xattn_o": inputs["xattn_w_o"][0],
        "ffn2_gate": inputs["ffn2_w_gate"][0], "ffn2_up": inputs["ffn2_w_up"][0],
        "ffn2_down": inputs["ffn2_w_down"][0],
    }
    arrays = {f"{n}_dram": np.ascontiguousarray(a) for n, a in arrays.items()}
    nc = bacc.Bacc("TRN2", target_bir_lowering=False, num_devices=1)
    args = [nc.dram_tensor(n, a.shape, mybir.dt.from_np(a.dtype), kind="ExternalInput").ap()
            for n, a in arrays.items()]
    out = nc.dram_tensor("out_dram", inputs["x"].shape[1:], mybir.dt.float32, kind="ExternalOutput").ap()
    build_program(nc, *args, out)
    r = run_bass_kernel_spmd(nc, [arrays], core_ids=[0])
    return r.results[0]["out_dram"].reshape(inputs["x"].shape)
```
